# Optimizing a Trainium2 kernel written in Bass

```python
import jax
import jax.numpy as jnp
from jax import lax
import numpy as np

D_MODEL = 1024
BATCH = 1
SEQ = 256
DEPTH = 2

HGRN_HEADS = 4
HGRN_DIM = 128
HGRN_WIDTH = HGRN_HEADS * HGRN_DIM
RET_HEADS = 4
RET_DIM = 128
RET_WIDTH = RET_HEADS * RET_DIM
SWA_Q_HEADS = 8
SWA_KV_HEADS = 2
SWA_DIM = 64
SWA_Q_WIDTH = SWA_Q_HEADS * SWA_DIM
SWA_KV_WIDTH = SWA_KV_HEADS * SWA_DIM
WINDOW = 128
SWA_BLOCK = 128
N_BRANCHES = 3
CHUNK = 64
ROPE_THETA = 10000.0
N_MEM = 256
X_HEADS = 4
X_DIM = D_MODEL // X_HEADS
PEER_HEADS = 8
PEER_N_KEYS = 128
PEER_N_EXPERTS = PEER_N_KEYS * PEER_N_KEYS
PEER_TOPK = 16
PEER_QDIM = 256
PEER_HALF = PEER_QDIM // 2
PEER_TOK_BLOCK = 128
EPS = 1e-6
NEG_BIG = -1e30
TINY = 1e-30

IN_SIZES = (HGRN_WIDTH,) * 4 + (RET_WIDTH,) * 4 + (SWA_Q_WIDTH, SWA_KV_WIDTH, SWA_KV_WIDTH, N_BRANCHES * D_MODEL)
IN_COLS = int(sum(IN_SIZES))
IN_SPLITS = tuple(int(c) for c in np.cumsum(IN_SIZES)[:-1])

kernel_name = 'hybrid_hgrn2_retnet_swa_peer'

def rmsnorm(x, g):
    xf = x.astype(jnp.float32)
    y = xf * lax.rsqrt(jnp.mean(xf * xf, axis=-1, keepdims=True) + EPS)
    if g is not None:
        y = y * g.astype(jnp.float32)
    return y.astype(x.dtype)

def rope(a, pos, inv_freq):
    ang = pos.astype(jnp.float32)[:, :, None, None] * inv_freq
    cos, sin = jnp.cos(ang), jnp.sin(ang)
    a1, a2 = jnp.split(a.astype(jnp.float32), 2, axis=-1)
    return jnp.concatenate([a1 * cos - a2 * sin, a2 * cos + a1 * sin], axis=-1).astype(a.dtype)

def split_heads(a, n):
    return a.reshape(a.shape[0], a.shape[1], n, -1)

def bhtd(a):
    return jnp.swapaxes(a, 1, 2)

def to_chunks(a):
    b, h, t, d = a.shape
    return jnp.moveaxis(a.reshape(b, h, t // CHUNK, CHUNK, d), 2, 0)

def from_chunks(a):
    n, b, h, c, d = a.shape
    return jnp.moveaxis(a, 0, 2).reshape(b, h, n * c, d)

def hgrn2_chunkwise(q, k, v, log_f):
    f32 = jnp.float32
    b, h, t, dk = q.shape
    dv = v.shape[-1]
    causal = jnp.tril(jnp.ones((CHUNK, CHUNK), dtype=bool))[:, :, None]

    def step(state, inp):
        qc, kc, vc, gc = inp
        cum = jnp.cumsum(gc, axis=2)
        o_inter = jnp.einsum('bhtk,bhkv->bhtv', qc * jnp.exp(cum), state)
        rel = jnp.where(causal, cum[:, :, :, None, :] - cum[:, :, None, :, :], NEG_BIG)
        scores = jnp.einsum('bhtk,bhsk,bhtsk->bhts', qc, kc, jnp.exp(rel))
        o = o_inter + jnp.einsum('bhts,bhsv->bhtv', scores, vc)
        last = cum[:, :, -1:, :]
        state = jnp.exp(last[:, :, 0, :, None]) * state + jnp.einsum('bhsk,bhsv->bhkv', kc * jnp.exp(last - cum), vc)
        return state, o

    s0 = jnp.zeros((b, h, dk, dv), f32)
    xs = tuple(to_chunks(a.astype(f32)) for a in (q, k, v, log_f))
    _, o = lax.scan(step, s0, xs)
    return from_chunks(o).astype(q.dtype)

def retention_chunkwise(q, k, v, log_gamma):
    f32 = jnp.float32
    b, h, t, dk = q.shape
    dv = v.shape[-1]
    idx = jnp.arange(CHUNK, dtype=f32)
    rel = idx[:, None] - idx[None, :]
    decay = jnp.exp(jnp.where(rel >= 0, log_gamma[:, None, None] * rel, NEG_BIG))
    q_decay = jnp.exp(log_gamma[:, None] * (idx + 1.0))[:, :, None]
    k_decay = jnp.exp(log_gamma[:, None] * (CHUNK - 1.0 - idx))[:, :, None]
    c_decay = jnp.exp(log_gamma * CHUNK)[:, None, None]

    def step(state, inp):
        qc, kc, vc = inp
        o_inter = jnp.einsum('bhtk,bhkv->bhtv', qc, state) * q_decay
        scores = jnp.einsum('bhtk,bhsk->bhts', qc, kc) * decay
        o = o_inter + jnp.einsum('bhts,bhsv->bhtv', scores, vc)
        state = c_decay * state + jnp.einsum('bhsk,bhsv->bhkv', kc * k_decay, vc)
        return state, o

    s0 = jnp.zeros((b, h, dk, dv), f32)
    xs = tuple(to_chunks(a.astype(f32)) for a in (q, k, v))
    _, o = lax.scan(step, s0, xs)
    return from_chunks(o).astype(q.dtype)

def swa_sink_attention(q, k, v, sinks):
    f32 = jnp.float32
    b, hq, t, dh = q.shape
    hkv = k.shape[1]
    g = hq // hkv
    nb = t // SWA_BLOCK
    qb = q.reshape(b, hkv, g, nb, SWA_BLOCK, dh)

    def band(a):
        ab = a.reshape(b, hkv, nb, SWA_BLOCK, dh)
        prev = jnp.pad(ab, ((0, 0), (0, 0), (1, 0), (0, 0), (0, 0)))[:, :, :-1]
        return jnp.concatenate([prev, ab], axis=3)

    kw, vw = band(k), band(v)
    s = jnp.einsum('bhgnqd,bhnkd->bhgnqk', qb, kw).astype(f32) * (dh ** -0.5)
    qi = jnp.arange(SWA_BLOCK)[:, None] + SWA_BLOCK
    ki = jnp.arange(2 * SWA_BLOCK)[None, :]
    rel = qi - ki
    in_window = (rel >= 0) & (rel < WINDOW)
    has_prev = (jnp.arange(nb) > 0)[:, None, None] | (ki >= SWA_BLOCK)[None]
    s = jnp.where(in_window[None] & has_prev, s, NEG_BIG)
    sink = sinks.astype(f32).reshape(1, hkv, g, 1, 1, 1)
    m = jnp.maximum(jnp.max(s, axis=-1, keepdims=True), sink)
    p = jnp.exp(s - m)
    denom = jnp.sum(p, axis=-1, keepdims=True) + jnp.exp(sink - m)
    o = jnp.einsum('bhgnqk,bhnkd->bhgnqd', p / denom, vw.astype(f32))
    return o.reshape(b, hq, t, dh).astype(q.dtype)

def memory_cross_attention(h, m, wq, wk, wv, wo):
    b, t, d = h.shape
    nm = m.shape[1]
    q = (h @ wq).reshape(b, t, X_HEADS, X_DIM)
    k = (m @ wk).reshape(b, nm, X_HEADS, X_DIM)
    v = (m @ wv).reshape(b, nm, X_HEADS, X_DIM)
    s = jnp.einsum('bthd,bmhd->bhtm', q, k).astype(jnp.float32) * (X_DIM ** -0.5)
    p = jax.nn.softmax(s, axis=-1)
    o = jnp.einsum('bhtm,bmhd->bthd', p, v.astype(jnp.float32)).reshape(b, t, d).astype(h.dtype)
    return o @ wo

def peer_ffn(h, wq, sub_keys, u_tab, v_tab):
    f32 = jnp.float32
    b, t, d = h.shape
    q = (h @ wq).reshape(b, t, PEER_HEADS, 2, PEER_HALF)
    s = jnp.einsum('bthpd,phnd->bthpn', q, sub_keys).astype(f32)
    sv, si = lax.top_k(s, PEER_TOPK)
    cand = (sv[..., 0, :, None] + sv[..., 1, None, :]).reshape(b, t, PEER_HEADS, PEER_TOPK * PEER_TOPK)
    cv, ci = lax.top_k(cand, PEER_TOPK)
    e1 = jnp.take_along_axis(si[..., 0, :], ci // PEER_TOPK, axis=-1)
    e2 = jnp.take_along_axis(si[..., 1, :], ci % PEER_TOPK, axis=-1)
    n_blk = (b * t) // PEER_TOK_BLOCK
    n_sel = PEER_HEADS * PEER_TOPK
    idx = (e1 * PEER_N_KEYS + e2).reshape(n_blk, PEER_TOK_BLOCK, n_sel)
    gate = jax.nn.softmax(cv, axis=-1).reshape(n_blk, PEER_TOK_BLOCK, n_sel)
    hb = h.reshape(n_blk, PEER_TOK_BLOCK, d)

    def block(args):
        hh, ii, gg = args
        act = jax.nn.gelu(jnp.einsum('td,ted->te', hh, u_tab[ii]).astype(f32), approximate=False)
        return jnp.einsum('te,ted->td', gg * act, v_tab[ii].astype(f32)).astype(hh.dtype)

    return lax.map(block, (hb, idx, gate)).reshape(b, t, d)

def setup_inputs(seed: int = 0) -> dict:
    key = jax.random.key(seed)
    ks = jax.random.split(key, 24)
    f32 = jnp.float32
    nrm = lambda k, shape, scale: jax.random.normal(k, shape, f32) * scale
    gain = lambda k, shape: 1.0 + 0.02 * jax.random.normal(k, shape, f32)
    offset = jax.random.randint(ks[2], (BATCH, 1), 0, 4096, dtype=jnp.int32)
    positions = offset + jnp.arange(SEQ, dtype=jnp.int32)[None, :]
    return {
        'x': nrm(ks[0], (BATCH, SEQ, D_MODEL), 1.0),
        'mem': nrm(ks[1], (BATCH, N_MEM, D_MODEL), 1.0),
        'positions': positions,
        'ln_mix': gain(ks[3], (DEPTH, D_MODEL)),
        'w_in': nrm(ks[4], (DEPTH, D_MODEL, IN_COLS), D_MODEL ** -0.5),
        'lb_param': nrm(ks[5], (DEPTH, HGRN_WIDTH), 1.0),
        'hgrn_norm': gain(ks[6], (DEPTH, HGRN_WIDTH)),
        'swa_sinks': nrm(ks[7], (DEPTH, SWA_Q_HEADS), 0.5),
        'w_br_hgrn': nrm(ks[8], (DEPTH, HGRN_WIDTH, D_MODEL), HGRN_WIDTH ** -0.5),
        'w_br_ret': nrm(ks[9], (DEPTH, RET_WIDTH, D_MODEL), RET_WIDTH ** -0.5),
        'w_br_swa': nrm(ks[10], (DEPTH, SWA_Q_WIDTH, D_MODEL), SWA_Q_WIDTH ** -0.5),
        'w_out': nrm(ks[11], (DEPTH, D_MODEL, D_MODEL), D_MODEL ** -0.5),
        'ln_xq': gain(ks[12], (DEPTH, D_MODEL)),
        'ln_xkv': gain(ks[13], (DEPTH, D_MODEL)),
        'w_xq': nrm(ks[14], (DEPTH, D_MODEL, D_MODEL), D_MODEL ** -0.5),
        'w_xk': nrm(ks[15], (DEPTH, D_MODEL, D_MODEL), D_MODEL ** -0.5),
        'w_xv': nrm(ks[16], (DEPTH, D_MODEL, D_MODEL), D_MODEL ** -0.5),
        'w_xo': nrm(ks[17], (DEPTH, D_MODEL, D_MODEL), D_MODEL ** -0.5),
        'ln_ffn': gain(ks[18], (DEPTH, D_MODEL)),
        'peer_wq': nrm(ks[19], (DEPTH, D_MODEL, PEER_HEADS * PEER_QDIM), D_MODEL ** -0.5),
        'peer_keys': nrm(ks[20], (DEPTH, 2, PEER_HEADS, PEER_N_KEYS, PEER_HALF), PEER_HALF ** -0.5),
        'peer_u': nrm(ks[21], (DEPTH, PEER_N_EXPERTS, D_MODEL), D_MODEL ** -0.5),
        'peer_v': nrm(ks[22], (DEPTH, PEER_N_EXPERTS, D_MODEL), PEER_HEADS ** -0.5),
        'ln_final': gain(ks[23], (D_MODEL,)),
    }

def reference(x, mem, positions, ln_mix, w_in, lb_param, hgrn_norm, swa_sinks, w_br_hgrn, w_br_ret, w_br_swa, w_out, ln_xq, ln_xkv, w_xq, w_xk, w_xv, w_xo, ln_ffn, peer_wq, peer_keys, peer_u, peer_v, ln_final):
    f32 = jnp.float32
    b, t, d = x.shape
    swa_inv_freq = ROPE_THETA ** (-jnp.arange(0, SWA_DIM, 2, dtype=f32) / SWA_DIM)
    ret_inv_freq = ROPE_THETA ** (-jnp.linspace(0.0, 1.0, RET_DIM // 2, dtype=f32))
    log_gamma = jnp.log(1.0 - 2.0 ** (-5.0 - jnp.arange(RET_HEADS, dtype=f32)))
    lb_sm = jax.nn.softmax(lb_param.astype(f32), axis=0)
    lower = jnp.cumsum(lb_sm, axis=0) - lb_sm[0]

    for l in range(DEPTH):
        h = rmsnorm(x, ln_mix[l])
        (hq, hf, hi, hg, rq, rk, rv, rg, sq, sk, sv, gate_logits) = jnp.split(h @ w_in[l], IN_SPLITS, axis=-1)

        lb = lower[l]
        z = hf.astype(f32)
        f_gate = lb + (1.0 - lb) * jax.nn.sigmoid(z)
        log_f = jnp.log(jnp.maximum(f_gate, TINY))
        k_in = (1.0 - lb) * jax.nn.sigmoid(-z)
        qa = bhtd(split_heads(jax.nn.silu(hq), HGRN_HEADS)) * (HGRN_DIM ** -0.5)
        oa = hgrn2_chunkwise(qa, bhtd(split_heads(k_in, HGRN_HEADS)), bhtd(split_heads(hi, HGRN_HEADS)), bhtd(split_heads(log_f, HGRN_HEADS)))
        oa = rmsnorm(bhtd(oa).reshape(b, t, HGRN_WIDTH), hgrn_norm[l]) * jax.nn.silu(hg)
        y_a = oa @ w_br_hgrn[l]

        qb = bhtd(rope(split_heads(rq, RET_HEADS), positions, ret_inv_freq))
        kb = bhtd(rope(split_heads(rk, RET_HEADS), positions, ret_inv_freq)) * (RET_DIM ** -0.5)
        ob = retention_chunkwise(qb, kb, bhtd(split_heads(rv, RET_HEADS)), log_gamma)
        ob = rmsnorm(bhtd(ob), None).reshape(b, t, RET_WIDTH) * jax.nn.silu(rg)
        y_b = ob @ w_br_ret[l]

        qc = bhtd(rope(split_heads(sq, SWA_Q_HEADS), positions, swa_inv_freq))
        kc = bhtd(rope(split_heads(sk, SWA_KV_HEADS), positions, swa_inv_freq))
        oc = swa_sink_attention(qc, kc, bhtd(split_heads(sv, SWA_KV_HEADS)), swa_sinks[l])
        y_c = bhtd(oc).reshape(b, t, SWA_Q_WIDTH) @ w_br_swa[l]

        gates = jax.nn.sigmoid(gate_logits.reshape(b, t, N_BRANCHES, d))
        mixed = gates[:, :, 0] * y_a + gates[:, :, 1] * y_b + gates[:, :, 2] * y_c
        x = x + mixed @ w_out[l]

        x = x + memory_cross_attention(rmsnorm(x, ln_xq[l]), rmsnorm(mem, ln_xkv[l]), w_xq[l], w_xk[l], w_xv[l], w_xo[l])

        x = x + peer_ffn(rmsnorm(x, ln_ffn[l]), peer_wq[l], peer_keys[l], peer_u[l], peer_v[l])

    return rmsnorm(x, ln_final)


_drawn_inputs = setup_inputs


def setup_inputs(seed=0):
    import zlib

    import numpy as np

    out = dict(_drawn_inputs(seed))
    spreads = {}
    factors = {'swa_sinks': 4.165, 'ln_xq': 3.651, 'ln_xkv': 3.042, 'ln_final': 2.904}
    for name, (base, spread) in spreads.items():
        noise = np.random.default_rng([zlib.crc32(name.encode()), seed]).standard_normal(out[name].shape)
        drawn = base * np.exp(spread * noise) if base else spread * noise
        out[name] = jnp.asarray(drawn.astype(out[name].dtype))
    for name, factor in factors.items():
        out[name] = (out[name] * factor).astype(out[name].dtype)
    return out
```

```python
from contextlib import ExitStack

import numpy as np

import concourse.bass as bass
from concourse import mybir

ALU = mybir.AluOpType
ACT = mybir.ActivationFunctionType
AX = mybir.AxisListType
F32 = mybir.dt.float32
F32R = mybir.dt.float32r
BF16 = mybir.dt.bfloat16
I32 = mybir.dt.int32
U32 = mybir.dt.uint32

P = 128
D = 1024
KC = D // P
T = 256
NT = T // P
DEPTH = 2
EPS = 1e-6
TINY = 1e-30
NEG_BIG = -1e30
HEADS = 4
SWA_DIM = 64
N_MEM = 256
XH = 4
PH = 8
TOPK = 16
NK = 128
QUARTERS = 4
QB = NK // QUARTERS
TOK = T // QB
SLOTS = 4

G_RQ, G_RK, G_RV, G_RG, G_SQ, G_SKV, G_HF, G_HQ, G_HI, G_HG = range(10)
G_GATE = 10
G_BR = 16
G_OUT, G_XK, G_XQ, G_XV, G_XO = 19, 21, 23, 25, 27
G_WQ = 29
G_AHEAD = 33
G_MAIN = G_AHEAD + QB // SLOTS
N_MAIN = (NK - QB) // 2
G_TAIL = G_MAIN + N_MAIN
GROUPS = G_TAIL + QB // SLOTS

T_RQ, T_RV, T_RG, T_SQ, T_SKV, T_HF, T_HQ, T_HI, T_HG, T_GATE = 0, 8, 12, 16, 20, 24, 28, 32, 36, 40
T_BR, T_OUT, T_XK, T_XQ, T_XV, T_XO, T_WQ, TILES = 64, 76, 84, 92, 100, 108, 116, 132

P_RV, P_SV, P_HI, P_XV, PAIRS = 0, 2, 3, 5, 9

SQUARES = KC // 2 + 1 + KC

GATES_OF = (KC, 2 * KC, 0)

LEVELS = (0, 1, 2, 4, 8, 16, 32, 64, 128)
CHAIN = 151


def lay_constants():
    f = np.float32
    lin = np.arange(64, dtype=f) * (f(1) / f(63))
    lin[-1] = 1
    ret = (10000.0 ** (-lin.astype(np.float64))).astype(f)
    swa = (10000.0 ** (-np.arange(0, SWA_DIM, 2) / SWA_DIM)).astype(f)
    freq = np.stack([np.tile(ret, 2), np.tile(swa, 4)], 1)

    def rotation(dim):
        r = np.zeros((P, P), f)
        for p in range(P):
            half = (p % dim) < dim // 2
            r[p + dim // 2 if half else p - dim // 2, p] = -1.0 if half else 1.0
        return r

    rot = np.stack([rotation(P), rotation(SWA_DIM)], 1)
    s = np.arange(P)[:, None]
    t = np.arange(P)[None, :]
    gamma = np.log(1.0 - 2.0 ** (-5.0 - np.arange(HEADS)))
    decay = np.zeros((P, HEADS, 3 * P))
    for h in range(HEADS):
        decay[:, h, 0:P] = np.where(t >= s, np.exp(gamma[h] * (t - s)), 0)
        decay[:, h, P:2 * P] = np.exp(gamma[h] * (t + P - s))
        decay[:, h, 2 * P:] = decay[:, h, 0:P]
    decay *= P ** -0.5
    level = np.zeros((P, 7, P), np.int32)
    for i, m in enumerate(LEVELS[1:8]):
        level[:, i] = (s // (2 * m) == t // (2 * m)) & ((s // m) % 2 == 0) & ((t // m) % 2 == 1)
    window = np.zeros((P, 3 * P), f)
    window[:, 0:P] = np.where(t <= s, 0, NEG_BIG)
    window[:, P:2 * P] = np.where(t > s, 0, NEG_BIG)
    window[:, 2 * P:] = window[:, 0:P]
    return {
        "c_freq": freq, "c_rot": rot, "c_decay": decay.astype(f), "c_level": level, "c_window": window,
        "c_ident": np.eye(P, dtype=f), "c_iota": np.broadcast_to(np.arange(P, dtype=f), (P, P)).copy(),
    }


def build(nc, a):
    ctx = ExitStack()
    with ctx:
        def sb(name, shape, dt=F32):
            return ctx.enter_context(nc.sbuf_tensor(name, shape, dt))

        sems = {}

        def sem(name):
            if name not in sems:
                sems[name] = ctx.enter_context(nc.semaphore(name))
            return sems[name]

        x = sb("x", [P, KC, T])
        ring = sb("ring", [P, SLOTS, D])
        w_hi = sb("w_hi", [P, SLOTS, D], F32R)
        w_lo = sb("w_lo", [P, SLOTS, D], F32R)
        h_r = sb("h_r", [P, 2, KC, T], F32R)
        o_r = sb("o_r", [P, 6144], F32R)
        hot_rows = sb("hot_rows", [P, TOK * (2 * QB + 2 * P + 6 * QB)], BF16)
        gate3 = sb("gate3", [P, T, 3], BF16)
        pair12 = sb("pair12", [P, 2, T], BF16)
        freq = sb("freq", [P, 2])
        ident = sb("ident", [P, P])
        iota = sb("iota", [P, P], BF16)
        ones = sb("ones", [P, P])
        zeros = sb("zeros", [P, P], BF16)
        smalls = sb("smalls", [P, DEPTH, 44])
        small = sb("small", [P, 44])
        gains = {"mix": 0, "xq": 8, "xkv": 16, "ffn": 24}
        hgain = small[:, 32:36]
        sink = small[:, 36:44]
        lower_all = sb("lower_all", [P, DEPTH, HEADS])
        low = sb("low", [P, HEADS])
        oml = sb("oml", [P, HEADS])
        gfin = sb("gfin", [P, KC])
        eps = sb("eps", [P, 1])
        rinv = sb("rinv", [P, T])
        minv = sb("minv", [P, N_MEM])
        negm = sb("negm", [P, 8])
        mx = sb("mx", [P, 8])
        rsum = sb("rsum", [P, 8])
        esink = sb("esink", [P, 8])
        arena = sb("arena", [P, 24832])

        def part(at, *shape, dt=F32, of=arena):
            n = int(np.prod(shape)) // (2 if dt is BF16 else 1)
            v = of[:, at:at + n]
            if of is arena and dt is not F32:
                v = v.bitcast(dt)
            if len(shape) == 1:
                return v
            names = "abcd"[:len(shape)]
            return v.rearrange(f"p ({' '.join(names)}) -> p {' '.join(names)}",
                               **{k: n for k, n in zip(names, shape)})

        def hotv(at, *shape):
            names = "abcd"[:len(shape)]
            return hot_rows[:, at:at + int(np.prod(shape))].rearrange(
                f"p ({' '.join(names)}) -> p {' '.join(names)}", **{k: n for k, n in zip(names, shape)})

        rq = part(0, HEADS, T)
        rk = part(1024, HEADS, T)
        rtmp = part(2048, HEADS, T)
        st = part(3072, HEADS, 3 * P)
        rv = part(4608, NT, 512)
        rg = part(5632, HEADS, T)
        rgs = part(6656, HEADS, T)
        hf = part(7680, HEADS, T)
        hq = part(8704, HEADS, T)
        hi = part(9728, NT, 512)
        hg = part(10752, HEADS, T)
        wqk = part(11776, 5, T)
        wtmp = part(13056, 5, T)
        wv = part(14336, NT, P)
        gates = part(14592, 24, T)
        decay = part(20736, HEADS, 3 * P)
        level_mask = part(22272, 7, P, dt=I32)
        window = part(23168, 3 * P)
        cosb = part(23552, 2, T)
        sinb = part(24064, 2, T)
        posf = part(2048, T)
        ang = part(2304, T)
        turn = part(2560, T)
        red = part(2816, T)
        posi = part(2816, T, dt=I32)
        rot = part(24576, 2, P)
        rrms = rq
        wp = st
        wpt = part(0, 4, 3 * P)
        cum = part(4608, 4 * T)
        kin = part(5632, 4 * T)
        hgs = rgs
        qin = part(13056, 4 * T)
        left = part(0, 4 * T)
        right = part(1024, 4 * T)
        span = part(2048, 4 * T)
        small_f = part(8704, 4 * T)
        hgo = part(2048, HEADS, T)
        mixed = part(0, KC, T)
        square = part(14592, KC, T)
        h = part(16640, KC, T)
        xq = part(0, KC, T)
        xp = part(2048, 8, N_MEM)
        xpt = part(4096, XH, 2, T)
        mem = part(7680, KC, N_MEM)
        kT = part(11776, KC, N_MEM)
        xv = part(18688, NT, D)
        keys = part(20736, 2 * PH, NK)
        pq = part(0, 2 * SLOTS, T)
        best = part(2048, NT, PH, 2, TOPK)
        idx = part(2560, NT, PH, 2, TOPK, dt=U32)
        idxb = part(3072, NT, PH, 2, TOPK, dt=BF16)
        kscore = part(4096, 2, NT, SLOTS, NK)
        work = part(8192, NT, SLOTS, NK)
        cand = part(8192, PH, TOPK * TOPK)
        candw = part(10240, PH, TOPK * TOPK)
        hot = part(12288, P, TOPK, dt=BF16)
        cidx = part(13952, PH, TOPK, dt=U32)
        cij = part(14080, 2, P, dt=U32)
        cijb = part(14336, 2, P, dt=BF16)
        cbest = part(14464, NT, PH, TOPK)
        sel = part(14720, NT, 3, P)
        gsum = part(15488, NT, PH)
        G = part(0, 2 * QB, T)
        actv = part(16384, QB, T)
        selT = part(12288, 3, T)
        product = part(24576, T)

        iota_f = part(0, P)
        lbp = part(P, DEPTH, HEADS)

        branch_r = [part(0, 3, HEADS, T, of=o_r), part(3072, 3, HEADS, T, of=o_r)]
        mn_r = [part(0, KC, N_MEM, of=o_r), part(2048, KC, N_MEM, of=o_r)]
        xo_r = mn_r
        hr = [h_r[:, 0], h_r[:, 1]]
        gated_r = [part(0, 2, T, of=o_r), part(512, 2, T, of=o_r)]
        equal2 = hotv(0, 2, TOK, QB)
        one1 = hotv(2 * TOK * QB, 2, TOK, P)
        one2 = hotv(2 * TOK * (QB + P), 2, TOK, 3, QB)

        bank = ctx.enter_context(nc.psum_tensor("banks", [P, 8, 512], F32))
        four = bank[:, 0:4, :]

        def pview(b, banks, pattern, **k):
            return bank[:, b:b + banks, :].rearrange("p b n -> p (b n)").rearrange(pattern, **k)

        def tile_out(n):
            return bank[:, 4 + n % 2, 0:T]

        def bc(ap, axis, n):
            s = list(ap.shape)
            s.insert(axis, n)
            return ap.unsqueeze(axis).to_broadcast(s)

        def loaded(eng, g, s):
            eng.wait_ge(sem(f"slot{s}_loaded"), (g + 1) * 16)

        def used(eng, g, s):
            eng.wait_ge(sem(f"slot{s}_used"), g + 2)

        block = ctx.enter_context(nc.Block())

        @block.sync
        def _(sp):
            for dst, src in ((x[:, :, :], a["x"]), (mem, a["mem"]), (smalls[:, :, :], a["small"]),
                             (lbp, a["lb"]), (gfin[:, :], a["gfin"]), (freq[:, :], a["c_freq"]), (ident[:, :], a["c_ident"]), (iota_f, a["c_iota"])):
                sp.dma_start(dst, src).then_inc(sem("consts"), 16)

            def load(g, s):
                sp.dma_start(ring[:, s, :], a["stream"][bass.ds(g * SLOTS + s, 1)].rearrange("a p n -> (a p) n")
                             ).then_inc(sem(f"slot{s}_loaded"), 16)

            for s in range(SLOTS):
                load(0, s)
            with sp.Fori(1, DEPTH * GROUPS + 1) as g:
                for s in range(SLOTS):
                    sp.wait_ge(sem(f"low{s}"), g)
                    load(g, s)
            sp.wait_ge(sem("final"), KC)
            sp.dma_start(a["out"], h).then_inc(sem("stored"), 16)
            sp.wait_ge(sem("stored"), 16)

        N_CONST = 8 * 16

        @block.gpsimd
        def _(pool):
            def low_part(g, s):
                pool.wait_ge(sem(f"high{s}"), g + 1)
                pool.tensor_tensor(w_lo[:, s, :], ring[:, s, :], w_hi[:, s, :], ALU.subtract
                                   ).then_inc(sem(f"low{s}"), 1)

            for s in range(SLOTS):
                low_part(0, s)
            with pool.Fori(0, DEPTH) as l:
                with pool.Fori(1, G_MAIN) as g:
                    for s in range(SLOTS):
                        low_part(l * GROUPS + g, s)
                with pool.Fori(0, QB // 2) as i:
                    for r in range(2):
                        pool.wait_ge(sem("equal2"), l * NK + i * 2 + r + 1)
                        pool.tensor_tensor(one2[:, r, :, :, :], bc(equal2[:, r, :, :], 2, 3),
                                           bc(gate3[:, bass.ds((i * 2 + r) * TOK, TOK), :], 3, QB),
                                           ALU.mult).then_inc(sem("pool_rows"), 1)
                with pool.Fori(G_MAIN, GROUPS + 1) as g:
                    for s in range(SLOTS):
                        low_part(l * GROUPS + g, s)

        @block.tensor
        def _(pe):
            pe.wait_ge(sem("consts"), N_CONST)
            pe.wait_ge(sem("setup_dve"), 2)
            pe.sem_inc(sem("gated"), 1)
            pe.sem_inc(sem("spread"), 2)
            for s in range(SLOTS):
                pe.sem_inc(sem(f"slot{s}_used"), 1)

            def rms_sums(src, chunks, ready, at, out):
                pe.wait_ge(ready, at)
                for k in range(chunks):
                    m = pe.matmul(out, ones[:, :], src[:, k, :], start=(k == 0), stop=(k == chunks - 1))
                return m

            rms_sums(square, KC, sem("mem_squared"), 1, bank[:, 6, 0:T]).then_inc(sem("mem_summed"), 1)

            def rms_pairs(at):
                for k in range(KC):
                    if k % 2 == 0:
                        pe.wait_ge(sem("squared"), at + k // 2 + 1)
                    m = pe.matmul(bank[:, 6, 0:T], ones[:, :], square[:, k, :], start=(k == 0), stop=(k == KC - 1))
                m.then_inc(sem("summed"), 1)

            with pe.Fori(0, DEPTH) as l:
                def ev(name, n=1, per=1):
                    pe.wait_ge(sem(name), l * per + n)

                def settle():
                    pe.sem_inc(sem("pe_settled"), 1)

                def wait_tile(g, s):
                    pe.wait_ge(sem(f"low{s}"), l * GROUPS + g + 1)

                def bank_free(n):
                    pe.wait_ge(sem("bank_free"), l * TILES + n + 1)

                def all_free(n):
                    pe.wait_ge(sem("bank_free"), l * TILES + n + 2)

                def product3(out, lhs, rhs, first, last):
                    pe.matmul(out, lhs[0], rhs[0], start=first, stop=False)
                    pe.matmul(out, lhs[0], rhs[1], start=False, stop=False)
                    return pe.matmul(out, lhs[1], rhs[0], start=False, stop=last)

                def weights(s, k):
                    return [w[:, s, k * P:(k + 1) * P] for w in (w_hi, w_lo)]

                def feature_tile(g, s, n, src, norm=None):
                    wait_tile(g, s)
                    bank_free(n)
                    for k in range(KC):
                        if norm is not None:
                            ev("h_ready", norm * KC + k + 1, 3 * KC)
                        m = product3(tile_out(s), weights(s, k), [v[:, k, :] for v in src], k == 0, k == KC - 1)
                    m.then_inc(sem(f"slot{s}_used"), 1)

                def token_pair(g, s, n, src):
                    wait_tile(g, s)
                    wait_tile(g, s + 1)
                    for t in range(NT):
                        bank_free(n + t)
                        for k in range(KC):
                            m = product3(tile_out(t).rearrange("p (a n) -> p a n", a=2),
                                         [v[:, k, t * P:(t + 1) * P] for v in src],
                                         [w[:, s:s + 2, k * P:(k + 1) * P] for w in (w_hi, w_lo)], k == 0, k == KC - 1)
                        m.then_inc(sem("token_half") if t == 0 else sem(f"slot{s}_used"), 1)

                def token_group(g, n, src):
                    for s in (0, 2):
                        token_pair(g, s, n + s, src)

                def group(g, n, tile, src):
                    for s in range(SLOTS):
                        tile(g, s, n + s, src)

                def groups(g0, count, n0, tile, src):
                    settle()
                    with pe.Fori(0, count) as i:
                        group(g0 + i, n0 + i * SLOTS, tile, src)

                rms_pairs(l * SQUARES)
                with pe.Fori(0, 2) as i:
                    for s in range(SLOTS):
                        feature_tile(G_RQ + i, s, T_RQ + i * SLOTS + s, hr, 0 if s == 0 else None)
                ev("rope_tables", 32, 32)
                all_free(T_RV)
                for n, src in enumerate((rq, rk)):
                    for j in range(2):
                        m = pe.matmul(bank[:, 2 * n + j, :], rot[:, 0, :], src[:, 2 * j:2 * j + 2, :],
                                      start=True, stop=True)
                    m.then_inc(sem("ret_rotated"), 1)
                token_group(G_RV, T_RV, hr)
                group(G_RG, T_RG, feature_tile, hr)
                ev("ret_roped")
                for hd in range(HEADS):
                    pe.matmul(bank[:, hd, 0:2 * P], rk[:, hd, 0:P], rq[:, hd, :], start=True, stop=True)
                    m = pe.matmul(bank[:, hd, 2 * P:3 * P], rk[:, hd, P:T], rq[:, hd, P:T], start=True, stop=True)
                m.then_inc(sem("ret_scored"), 1)
                group(G_SQ, T_SQ, feature_tile, hr)
                token_pair(G_SKV, 0, T_SKV, hr)
                feature_tile(G_SKV, 2, T_SKV + 2, hr)
                wait_tile(G_SKV, 3)
                pe.sem_inc(sem("slot3_used"), 1)

                def weighted(values, out0):
                    for hd in range(HEADS):
                        o = pview(out0, 2, "p (h t) -> p h t", h=HEADS)[:, hd, :]
                        v = values[:, :, hd * P:(hd + 1) * P]
                        pe.matmul(o[:, 0:P], v[:, 0, :], st[:, hd, 0:P], start=True, stop=True)
                        pe.matmul(o[:, P:T], v[:, 0, :], st[:, hd, P:2 * P], start=True, stop=False)
                        m = pe.matmul(o[:, P:T], v[:, 1, :], st[:, hd, 2 * P:3 * P], start=False, stop=True)
                    return m

                ev("ret_decayed")
                weighted(rv, 6).then_inc(sem("ret_summed"), 1)
                all_free(T_HF)
                for j in range(2):
                    pe.matmul(bank[:, j, :], rot[:, 1, :], wqk[:, 2 * j:2 * j + 2, :], start=True, stop=True)
                pe.matmul(bank[:, 2, 0:T], rot[:, 1, :], wqk[:, 4, :], start=True, stop=True
                          ).then_inc(sem("win_rotated"), 1)
                group(G_HF, T_HF, feature_tile, hr)
                ev("win_roped")
                ev("ret_squared")
                for j in range(2):
                    m = pe.matmul(bank[:, j, :], ones[:, :], rtmp[:, 2 * j:2 * j + 2, :], start=True, stop=True)
                m.then_inc(sem("ret_normsum"), 1)
                group(G_HQ, T_HQ, feature_tile, hr)

                def window_scores(half):
                    p0 = half * SWA_DIM
                    for j in range(4):
                        q = wqk[p0:p0 + SWA_DIM, j, :]
                        k = wqk[p0:p0 + SWA_DIM, 4, :]
                        pe.matmul(bank[:, j, 0:P], q[:, 0:P], k[:, 0:P], start=True, stop=True)
                        m = pe.matmul(bank[:, j, P:3 * P], q[:, P:T], k, start=True, stop=True)
                    m.then_inc(sem("win_scored"), 1)

                def window_turn(half):
                    ev("win_probs", half + 1, 2)
                    for j in range(4):
                        for n in range(3):
                            m = pe.transpose(bank[:, j, n * P:(n + 1) * P], wp[:, j, n * P:(n + 1) * P], ident[:, :])
                    m.then_inc(sem("win_turned"), 1)

                def window_values(half):
                    ev("win_turned_out", half + 1, 2)
                    p0 = half * SWA_DIM
                    o = pview(6, 2, "p (h t) -> p h t", h=4)
                    for j in range(4):
                        v = wv[:, :, p0:p0 + SWA_DIM]
                        pe.matmul(o[p0:p0 + SWA_DIM, j, 0:P], v[:, 0, :], wpt[:, j, 0:P], start=True, stop=True)
                        pe.matmul(o[p0:p0 + SWA_DIM, j, P:T], v[:, 0, :], wpt[:, j, P:2 * P], start=True, stop=False)
                        m = pe.matmul(o[p0:p0 + SWA_DIM, j, P:T], v[:, 1, :], wpt[:, j, 2 * P:3 * P],
                                      start=False, stop=True)
                    m.then_inc(sem("win_summed"), 1)

                ev("ret_rooted")
                window_scores(0)
                token_group(G_HI, T_HI, hr)
                window_turn(0)
                group(G_HG, T_HG, feature_tile, hr)
                ev("ret_out")
                window_values(0)
                window_scores(1)
                group(G_GATE, T_GATE, feature_tile, hr)
                window_turn(1)
                group(G_GATE + 1, T_GATE + 4, feature_tile, hr)
                window_values(1)

                def level(i, left=left, right=right):
                    ev("level_ready", i + 1, 9)
                    for j in range(HEADS * NT):
                        m = pe.matmul(pview(0, 2, "p (j t) -> p j t", j=8)[:, j, :], left[:, j * P:(j + 1) * P],
                                      right[:, j * P:(j + 1) * P], start=True, stop=True)
                    m.then_inc(sem("level_scored"), 1)

                def level_across():
                    ev("level_ready", 9, 9)
                    for hd in range(HEADS):
                        m = pe.matmul(bank[:, 2, hd * P:(hd + 1) * P], left[:, hd * T:hd * T + P],
                                      right[:, hd * T + P:(hd + 1) * T], start=True, stop=True)
                    m.then_inc(sem("level_scored"), 1)

                def gates_with_levels(i, last):
                    for s in range(SLOTS):
                        feature_tile(G_GATE + 2 + i, s, T_GATE + 8 + i * SLOTS + s, hr)
                        if s == 1:
                            level(2 * i + 1)
                    if last:
                        level_across()
                    else:
                        level(2 * i + 2)

                level(0, kin, qin)
                settle()
                with pe.Fori(0, 3) as i:
                    gates_with_levels(i, False)
                gates_with_levels(3, True)

                def branch_group(b, halfway=None):
                    if b == 0:
                        all_free(T_BR)
                    ev("branch_low", (1, 3, 4)[b], 4)
                    for s in range(SLOTS):
                        wait_tile(G_BR + b, s)
                        bank_free(T_BR + 4 * b + s)
                        for j in range(2):
                            for k in range(4):
                                m = product3(bank[:, 4 + s % 2, j * T:(j + 1) * T], weights(s, j * 4 + k),
                                             [v[:, b, k, :] for v in branch_r], k == 0, k == 3)
                        m.then_inc(sem(f"slot{s}_used"), 1)
                        if s == 1 and halfway:
                            halfway()

                branch_group(0)
                ev("hgrn_scores")
                ev("cross_out")
                weighted(hi, 6).then_inc(sem("hgrn_summed"), 1)
                branch_group(1, lambda: rms_sums(span.rearrange("p (h t) -> p h t", h=HEADS), HEADS, sem("hgrn_squared"),
                                                 l + 1, bank[:, 2, 0:T]).then_inc(sem("hgrn_normsum"), 1))
                branch_group(2)
                ev("mixed_low", 4, 4)
                groups(G_OUT, 2, T_OUT, feature_tile, hr)

                all_free(T_XK)
                ev("mn_low", KC, KC)
                group(G_XK, T_XK, feature_tile, mn_r)
                rms_sums(square, KC, sem("squared"), l * SQUARES + 5, bank[:, 6, 0:T]).then_inc(sem("summed"), 1)
                group(G_XK + 1, T_XK + 4, feature_tile, mn_r)
                ev("h_ready", 2 * KC, 3 * KC)
                groups(G_XQ, 2, T_XQ, feature_tile, hr)
                all_free(T_XV)
                xs = four.rearrange("p b (c m) -> p (b c) m", c=2)
                for hd in range(XH):
                    for t in range(NT):
                        for c in range(2):
                            m = pe.matmul(xs[:, hd * 2 + t, :], xq[:, hd * 2 + c, t * P:(t + 1) * P],
                                          kT[:, hd * 2 + c, :], start=(c == 0), stop=(c == 1))
                m.then_inc(sem("x_scored"), 1)
                settle()
                with pe.Fori(0, 2) as i:
                    token_group(G_XV + i, T_XV + i * SLOTS, mn_r)
                ev("x_probs")
                xt = four.rearrange("p b (c t) -> p b c t", c=2)
                for hd in range(XH):
                    for t in range(NT):
                        for c in range(2):
                            m = pe.transpose(xt[:, hd, c, t * P:(t + 1) * P],
                                             xp[:, hd * 2 + t, c * P:(c + 1) * P], ident[:, :])
                m.then_inc(sem("x_turned"), 1)
                ev("x_turned_out")
                all_free(T_XO)
                for k in range(KC):
                    for c in range(2):
                        m = pe.matmul(xs[:, k, :], xv[:, c, k * P:(k + 1) * P], xpt[:, k // 2, c, :],
                                      start=(c == 0), stop=(c == 1))
                m.then_inc(sem("x_summed"), 1)
                ev("xo_low")

                def square_sum(k):
                    pe.wait_ge(sem("squared"), l * SQUARES + 5 + k + 1)
                    return pe.matmul(bank[:, 6, 0:T], ones[:, :],
                                     square[:, k, :] if isinstance(k, int) else
                                     square[:, bass.ds(k, 1), :].rearrange("p a t -> p (a t)"),
                                     start=False, stop=True, skip_group_check=True)

                pe.matmul(bank[:, 6, 0:T], zeros[:, :], bc(zeros[:, :], 1, 2), start=True, stop=True)
                with pe.Fori(0, 2) as i:
                    for s in range(SLOTS):
                        feature_tile(G_XO + i, s, T_XO + i * SLOTS + s, xo_r)
                        if s:
                            square_sum(i * SLOTS + (s - 1))
                square_sum(SLOTS - 1)
                square_sum(KC - 1).then_inc(sem("summed"), 1)

                def key_scores(i, r):
                    pe.wait_ge(sem("bank_free"), l * TILES + T_WQ + (i * 2 + r + 1) * SLOTS + 2)
                    pe.wait_ge(sem("keys_out"), l * 4 + i * 2 + r + 1)
                    for t in range(NT):
                        for k in range(SLOTS):
                            m = pe.matmul(bank[:, 2 * r + t, k * P:(k + 1) * P],
                                          pq[:, r * SLOTS + k, t * P:(t + 1) * P],
                                          keys[:, bass.ds((i * 2 + r) * SLOTS + k, 1), :].rearrange("p a n -> p (a n)"),
                                          start=True, stop=True)
                    m.then_inc(sem("keys_scored"), 1)

                ev("keys_loaded", 16, 16)
                settle()
                with pe.Fori(0, 2) as i:
                    for r in range(2):
                        for k in range(SLOTS):
                            feature_tile(G_WQ + i * 2 + r, k, T_WQ + (i * 2 + r) * SLOTS + k, hr,
                                         2 if (r, k) == (0, 0) else None)
                            if (r, k) == (1, 1):
                                key_scores(i, 0)
                    key_scores(i, 1)

                def up(g, s, b, parity):
                    wait_tile(g, s)
                    pe.wait_ge(sem("up_free"), l * NK + b + 1)
                    for k in range(KC):
                        m = product3(tile_out(parity), weights(s, k), [v[:, k, :] for v in hr], k == 0, k == KC - 1)
                    m.then_inc(sem(f"slot{s}_used"), 1)

                settle()
                with pe.Fori(0, QB // SLOTS) as i:
                    for s in range(SLOTS):
                        up(G_AHEAD + i, s, i * SLOTS + s, s)
                ev("selected", NT, NT)
                for t in range(NT):
                    for n in range(3):
                        m = pe.transpose(bank[:, 6 + t, n * P:(n + 1) * P], sel[:, t, n, :], ident[:, :])
                    m.then_inc(sem("sel_turned"), 1)
                ev("keys_out", 6, 4)
                for b in range(4):
                    pe.matmul(bank[:, b, :], zeros[:, :], bc(zeros[:, :], 1, 4), start=True, stop=True)

                def spread(j, parity, shared=False):
                    pe.wait_ge(sem("hot_ready"), l * NK + j + 1)
                    if shared:
                        pe.wait_ge(sem("pool_rows"), l * QB + j + 1)
                    pe.wait_ge(sem("spread_free"), l * NK + j + 1)
                    for t in range(TOK):
                        o = bank[:, 6 + parity, t * QB:(t + 1) * QB]
                        for c in range(3):
                            m = pe.matmul(o, one1[:, parity, t, :], one2[:, parity, t, c, :],
                                          start=(c == 0), stop=(c == 2))
                    m.then_inc(sem("spread"), 1)

                settle()
                with pe.Fori(0, QB // 2) as i:
                    for r in range(2):
                        spread(i * 2 + r, r, shared=True)
                spread(QB, 0)

                y = four.rearrange("p b (c t) -> p (b c) t", c=2)

                def down(g, s, n, parity):
                    wait_tile(g, s)
                    pe.wait_ge(sem("gated"), l * NK + n + 2)
                    for k in range(KC):
                        w = weights(s, k)
                        for u, v in ((0, 0), (0, 1), (1, 0)):
                            m = pe.matmul(y[:, k, :], w[u], gated_r[v][:, parity, :], start=False, stop=True,
                                          skip_group_check=True)
                    m.then_inc(sem(f"slot{s}_used"), 1)

                def main(q, i, last):
                    n0 = q * QB + i * 2
                    g = G_MAIN + q * (QB // 2) + i
                    for r in range(2):
                        up(g, 2 * r, QB + n0 + r, r)
                        if not (q == QUARTERS - 2 and last and r):
                            spread(QB + 1 + n0 + r, 1 - r)
                        down(g, 2 * r + 1, n0 + r, r)

                settle()
                for q in range(QUARTERS - 1):
                    with pe.Fori(0, QB // 2 - 1) as i:
                        main(q, i, False)
                    main(q, QB // 2 - 1, True)
                with pe.Fori(0, QB // SLOTS) as i:
                    for s in range(SLOTS):
                        down(G_TAIL + i, s, NK - QB + i * SLOTS + s, s % 2)

            rms_pairs(DEPTH * SQUARES)

        @block.scalar
        def _(act):
            def high_part(g, s):
                loaded(act, g, s)
                act.activation(w_hi[:, s, :], ring[:, s, :], ACT.Copy).then_inc(sem(f"high{s}"), 1)

            act.wait_ge(sem("consts"), N_CONST)
            act.wait_ge(sem("setup_dve"), 2)
            act.activation(square, mem, ACT.Square).then_inc(sem("mem_squared"), 1)
            for s in range(SLOTS):
                high_part(0, s)
            act.wait_ge(sem("mem_summed"), 1)
            act.activation(minv[:, :], bank[:, 6, 0:T], ACT.Sqrt, bias=eps[:, :], scale=1.0 / D
                           ).then_inc(sem("mem_rooted"), 1)
            act.wait_ge(sem("lb_shifted"), 1)
            act.activation(lbp, lower_all[:, :, :], ACT.Exp).then_inc(sem("lb_exp"), 1)
            act.sem_inc(sem("bank_free"), 2)
            act.sem_inc(sem("up_free"), 2)
            act.sem_inc(sem("keys_out"), 2)
            act.sem_inc(sem("keys_read"), 2)
            act.sem_inc(sem("spread_free"), 2)

            def root(n):
                for k in range(0, KC, 2):
                    act.activation(square[:, k:k + 2, :], x[:, k:k + 2, :], ACT.Square).then_inc(sem("squared"), 1)
                take_root(n)

            def take_root(n):
                act.wait_ge(sem("summed"), n + 1)
                act.activation(rinv[:, :], bank[:, 6, 0:T], ACT.Sqrt, bias=eps[:, :], scale=1.0 / D
                               ).then_inc(sem("rooted"), 1)

            with act.Fori(0, DEPTH) as l:
                def ev(name, n=1, per=1):
                    act.wait_ge(sem(name), l * per + n)

                def copied(n):
                    act.wait_ge(sem("bank_free"), l * TILES + n + 2)

                def split_next(g, s):
                    used(act, l * GROUPS + g, s)
                    high_part(l * GROUPS + g + 1, s)

                def parts(src, dst, made, at, per, done):
                    ev(made, at, per)
                    act.activation(dst, src, ACT.Copy).then_inc(sem(done), 1)

                def high_parts(n):
                    for k in range(KC):
                        parts(h[:, k, :], hr[0][:, k, :], "h_made", n * KC + k + 1, 3 * KC, "h_high")

                ev("x_ready", 1, 3)
                for dst, src in ((posi, a["pos"].partition_broadcast(P).rearrange("p a t -> p (a t)")), (rot, a["c_rot"])):
                    act.dma_start(dst, src).then_inc(sem("rope_tables"), 16)
                for dst, src in ((decay, a["c_decay"]), (level_mask, a["c_level"]), (window, a["c_window"])):
                    act.dma_start(dst, src).then_inc(sem("tables"), 16)
                root(l * 3)
                high_parts(0)

                def evac(g, s, dst):
                    used(act, l * GROUPS + g, s)
                    act.activation(dst, tile_out(s).rearrange("p (a t) -> p a t", a=dst.shape[1]), ACT.Copy
                                   ).then_inc(sem("bank_free"), 1)
                    high_part(l * GROUPS + g + 1, s)

                def evac_group(g, out, n0=0):
                    for s in range(SLOTS):
                        evac(g, s, out(n0 + s))

                def evac_groups(g0, count, out):
                    with act.Fori(0, count) as i:
                        evac_group(g0 + i, out, i * SLOTS)

                def pass_group(g):
                    for s in range(SLOTS):
                        split_next(g, s)

                def by_feature(dst):
                    return lambda n: dst[:, bass.ds(n, 1), :]

                def evac_pair(g, s, pair, dst, cols=2 * P):
                    ev("token_half", pair + 1, PAIRS)
                    act.activation(dst(0), tile_out(0)[:, 0:cols], ACT.Copy).then_inc(sem("bank_free"), 1)
                    used(act, l * GROUPS + g, s)
                    act.activation(dst(1), tile_out(1)[:, 0:cols], ACT.Copy).then_inc(sem("bank_free"), 1)
                    act.sem_inc(sem(f"slot{s + 1}_used"), 1)
                    high_part(l * GROUPS + g + 1, s)
                    high_part(l * GROUPS + g + 1, s + 1)

                def evac_tokens(g, pair, dst, n0=0):
                    for s in (0, 2):
                        evac_pair(g, s, pair + s // 2,
                                  lambda t: dst[:, t, bass.ds((n0 + s) * P, 2 * P)])

                evac_groups(G_RQ, 2, by_feature(part(0, 8, T)))
                ev("angles", 4, 4)
                act.activation(sinb, sinb, ACT.Sin).then_inc(sem("trig"), 1)
                act.activation(cosb, cosb, ACT.Sin).then_inc(sem("trig"), 1)
                evac_tokens(G_RV, P_RV, rv)
                evac_group(G_RG, by_feature(rg))
                copied(T_SQ)
                act.activation(rgs, rg, ACT.Sigmoid).then_inc(sem("ret_sig"), 1)
                evac_group(G_SQ, by_feature(wqk))
                evac_pair(G_SKV, 0, P_SV, lambda t: wv[:, t, :], P)
                evac(G_SKV, 2, wqk[:, 4:5, :])
                split_next(G_SKV, 3)
                copied(T_SKV + 3)
                act.sem_inc(sem("bank_free"), 1)
                ev("ret_summed")
                ro = pview(6, 2, "p (h t) -> p h t", h=HEADS)
                act.activation(rtmp, ro, ACT.Square).then_inc(sem("ret_squared"), 1)
                evac_group(G_HF, by_feature(hf))
                ev("ret_normsum")
                act.activation(rrms, pview(0, 2, "p (h t) -> p h t", h=HEADS), ACT.Sqrt, bias=eps[:, :],
                               scale=1.0 / P).then_inc(sem("ret_rooted"), 1)
                evac_group(G_HQ, by_feature(hq))

                def window_exp(half):
                    ev("win_max", half + 1, 2)
                    for j in range(4):
                        for t, (c0, c1) in enumerate(((0, P), (P, 3 * P))):
                            c = j * 2 + t
                            act.activation(wp[:, j, c0:c1], wp[:, j, c0:c1], ACT.Exp, bias=negm[:, c:c + 1],
                                           accum_out=rsum[:, c:c + 1]).then_inc(sem("win_exp"), 1)
                    act.activation(esink[:, :], esink[:, :], ACT.Exp).then_inc(sem("win_exp"), 1)

                def window_turned(half):
                    ev("win_turned", half + 1, 2)
                    act.activation(wpt, bank[:, 0:4, 0:3 * P], ACT.Copy).then_inc(sem("win_turned_out"), 1)

                def window_out(half):
                    ev("win_summed", half + 1, 2)
                    p0 = half * SWA_DIM
                    act.activation(branch_r[0][p0:p0 + SWA_DIM, 1, :, :],
                                   pview(6, 2, "p (h t) -> p h t", h=4)[p0:p0 + SWA_DIM], ACT.Copy
                                   ).then_inc(sem("branch_high"), 1)

                parts(rrms, branch_r[0][:, 0, :, :], "ret_out", 1, 1, "branch_high")
                window_exp(0)
                evac_tokens(G_HI, P_HI, hi)
                window_turned(0)
                evac_group(G_HG, by_feature(hg))
                window_out(0)
                window_exp(1)
                evac_group(G_GATE, by_feature(gates))
                window_turned(1)
                copied(T_GATE)
                for n, (dst, src, scale) in enumerate(((cum, hf, 1.0), (kin, hf, -1.0), (qin, hq, 1.0), (hgs, hg, 1.0))):
                    if len(dst.shape) == 2:
                        src = src.rearrange("p h t -> p (h t)")
                    act.activation(dst, src, ACT.Sigmoid, scale=scale).then_inc(sem("hgrn_sig"), 1)
                evac_group(G_GATE + 1, by_feature(gates), 4)
                window_out(1)
                ev("forget")
                act.activation(cum, cum, ACT.Ln).then_inc(sem("log_forget"), 1)

                def level_exp(i):
                    m = LEVELS[i]
                    ev("span_ready", i, 8)
                    c = cum.rearrange("p (b s m) -> p b s m", s=2, m=m)
                    d = span.rearrange("p (b s m) -> p b s m", s=2, m=m)
                    act.activation(d[:, :, 0, :], d[:, :, 0, :], ACT.Exp).then_inc(sem("level_exp"), 1)
                    act.activation(d[:, :, 1, :], c[:, :, 1, :], ACT.Exp).then_inc(sem("level_exp"), 1)

                for i in range(4):
                    for s in range(SLOTS):
                        if s % 2 == 0:
                            level_exp(2 * i + 1 + s // 2)
                        evac(G_GATE + 2 + i, s, gates[:, bass.ds(8 + 4 * i + s, 1), :])
                copied(T_BR)

                def scores_across():
                    ev("level_scored", 9, 9)
                    act.activation(st[:, :, P:2 * P], bank[:, 2, :].rearrange("p (h t) -> p h t", h=HEADS), ACT.Copy
                                   ).then_inc(sem("cross_out"), 1)

                for g0 in GATES_OF:
                    act.activation(gates[:, g0:g0 + KC, :], gates[:, g0:g0 + KC, :], ACT.Sigmoid
                                   ).then_inc(sem("gates_ready"), 1)
                    if g0 == GATES_OF[0]:
                        scores_across()
                pass_group(G_BR)
                ev("hgrn_summed")
                act.dma_start(mem, a["mem"]).then_inc(sem("mem_loaded"), 16)
                act.activation(span.rearrange("p (h t) -> p h t", h=HEADS), ro, ACT.Square
                               ).then_inc(sem("hgrn_squared"), 1)
                split_next(G_BR + 1, 0)
                split_next(G_BR + 1, 1)
                ev("hgrn_normsum")
                act.activation(rinv[:, :], bank[:, 2, 0:T], ACT.Sqrt, bias=eps[:, :], scale=1.0 / 512
                               ).then_inc(sem("hgrn_rooted"), 1)
                split_next(G_BR + 1, 2)
                parts(hgo, branch_r[0][:, 2, :, :], "hgrn_out", 1, 1, "branch_high")
                split_next(G_BR + 1, 3)
                for s in range(SLOTS):
                    split_next(G_BR + 2, s)
                    parts(mixed[:, 2 * s:2 * s + 2, :], hr[0][:, 2 * s:2 * s + 2, :], "mixed_ready", SLOTS + s + 1,
                          2 * SLOTS, "mixed_high")
                for k in range(KC):
                    parts(mem[:, k, :], mn_r[0][:, k, :], "mn_made", k + 1, KC, "mn_high")
                pass_group(G_OUT)
                pass_group(G_OUT + 1)

                ev("x_ready", 2, 3)
                act.activation(square, x[:, :, :], ACT.Square).then_inc(sem("squared"), 1)
                evac_group(G_XK, by_feature(kT))
                act.wait_ge(sem("summed"), l * 3 + 2)
                act.activation(rinv[:, :], bank[:, 6, 0:T], ACT.Sqrt, bias=eps[:, :], scale=1.0 / D
                               ).then_inc(sem("rooted"), 1)
                for k in range(KC):
                    parts(h[:, k, :], hr[0][:, k, :], "h_made", KC + k + 1, 3 * KC, "h_high")
                act.dma_start(keys, a["keys"][bass.ds(l, 1)].rearrange("a p g n -> (a p) g n")
                              ).then_inc(sem("keys_loaded"), 16)
                evac_group(G_XK + 1, by_feature(kT), 4)
                evac_groups(G_XQ, 2, by_feature(xq))
                ev("x_max")
                xs = four.rearrange("p b (c m) -> p (b c) m", c=2)
                for c in range(8):
                    act.activation(xp[:, c, :], xs[:, c, :], ACT.Exp, bias=negm[:, c:c + 1],
                                   scale=(2 * P) ** -0.5, accum_out=rsum[:, c:c + 1]).then_inc(sem("x_exp"), 1)
                with act.Fori(0, 2) as i:
                    evac_tokens(G_XV + i, P_XV + i * 2, xv, i * SLOTS)
                ev("x_turned")
                act.activation(xpt, four.rearrange("p b (c t) -> p b c t", c=2), ACT.Copy
                               ).then_inc(sem("x_turned_out"), 1)
                ev("x_summed")
                act.activation(xo_r[0], xs, ACT.Copy).then_inc(sem("xo_high"), 1)
                for i in range(2):
                    for s in range(SLOTS):
                        split_next(G_XO + i, s)
                        act.wait_ge(sem("bank_free"), l * TILES + T_XO + i * SLOTS + s + 3)
                        act.activation(square[:, i * SLOTS + s, :], x[:, i * SLOTS + s, :], ACT.Square
                                       ).then_inc(sem("squared"), 1)

                take_root(l * 3 + 2)
                high_parts(2)
                with act.Fori(0, 2) as i:
                    def scores_out(r):
                        act.wait_ge(sem("keys_scored"), l * 4 + i * 2 + r + 1)
                        act.wait_ge(sem("keys_read"), l * 4 + i * 2 + r + 1)
                        act.activation(kscore[:, r], bank[:, 2 * r:2 * r + 2, :].rearrange("p t (k n) -> p t k n", k=SLOTS),
                                       ACT.Copy).then_inc(sem("keys_out"), 1)

                    evac_group(G_WQ + i * 2, by_feature(pq))
                    for k in range(SLOTS):
                        evac(G_WQ + i * 2 + 1, k, by_feature(pq)(SLOTS + k))
                        if k == 1:
                            scores_out(0)
                    scores_out(1)

                def gelu(g, s, parity, slot):
                    used(act, l * GROUPS + g, s)
                    act.activation(actv[:, slot, :] if isinstance(slot, int) else
                                   actv[:, bass.ds(slot, 1), :].rearrange("p a t -> p (a t)"),
                                   tile_out(parity), ACT.Gelu).then_inc(sem("up_free"), 1)
                    high_part(l * GROUPS + g + 1, s)

                with act.Fori(0, QB // SLOTS) as i:
                    for s in range(SLOTS):
                        gelu(G_AHEAD + i, s, s, i * SLOTS + s)
                ev("cand_max", NT, NT)
                act.activation(cbest, cbest, ACT.Exp).then_inc(sem("cand_exp"), 1)
                for t in range(NT):
                    ev("sel_turned", t + 1, 2)
                    act.activation(selT[:, :, t * P:(t + 1) * P],
                                   bank[:, 6 + t, 0:3 * P].rearrange("p (a t) -> p a t", a=3),
                                   ACT.Copy).then_inc(sem("sel_turned_out"), 1)

                def spread_out(j, parity, block0, tok0):
                    act.wait_ge(sem("spread"), l * NK + j + 3)
                    act.activation(G[:, block0:block0 + QB, bass.ds(tok0, TOK)],
                                   bank[:, 6 + parity, 0:T].rearrange("p (t b) -> p b t", t=TOK), ACT.Copy
                                   ).then_inc(sem("spread_free"), 1)

                def gated_high(m, parity):
                    act.wait_ge(sem("multiplied"), l * NK + m + 1)
                    act.activation(gated_r[0][:, parity, :], product, ACT.Copy
                                   ).then_inc(sem("gated_high"), 1)

                with act.Fori(0, QB // 2) as i:
                    for r in range(2):
                        spread_out(i * 2 + r, r, 0, (i * 2 + r) * TOK)
                spread_out(QB, 0, QB, 0)
                gated_high(0, 0)

                def main(q, i, last):
                    n0 = q * QB + i * 2
                    g = G_MAIN + q * (QB // 2) + i
                    for r in range(2):
                        act.wait_ge(sem("multiplied"), l * NK + n0 + r + 1)
                        gelu(g, 2 * r, r, i * 2 + r)
                        over = last and r == 1
                        if not (q == QUARTERS - 2 and over):
                            spread_out(QB + 1 + n0 + r, 1 - r, ((q if over else q + 1) % 2) * QB,
                                       0 if over else (i * 2 + r + 1) * TOK)
                        gated_high(n0 + r + 1, 1 - r)
                        split_next(g, 2 * r + 1)

                for q in range(QUARTERS - 1):
                    with act.Fori(0, QB // 2 - 1) as i:
                        main(q, i, False)
                    main(q, QB // 2 - 1, True)

                def tail(i, last):
                    for s in range(SLOTS):
                        if not (last and s == SLOTS - 1):
                            gated_high(NK - QB + i * SLOTS + s + 1, (s + 1) % 2)
                        split_next(G_TAIL + i, s)

                with act.Fori(0, QB // SLOTS - 1) as i:
                    tail(i, False)
                tail(QB // SLOTS - 1, True)
            act.wait_ge(sem("x_ready"), DEPTH * 3 + 1)
            root(DEPTH * 3)

        @block.vector
        def _(dve):
            chained = [0]

            def link(ins):
                chained[0] += 1
                ins.then_inc(sem("setup_chain"), 1)
                dve.wait_ge(sem("setup_chain"), chained[0])

            dve.sem_inc(sem("x_ready"), 1)
            dve.memset(eps[:, :], EPS)
            dve.memset(zeros[:, :], 0.0)
            dve.memset(ones[:, :], 1.0).then_inc(sem("setup_dve"), 1)
            dve.wait_ge(sem("consts"), N_CONST)
            dve.tensor_copy(iota[:, :], iota_f).then_inc(sem("setup_dve"), 1)

            top = low[:, :]
            link(dve.tensor_copy(top, lbp[:, 0, :]))
            for d in range(1, DEPTH):
                link(dve.tensor_tensor(top, top, lbp[:, d, :], ALU.max))
            for d in range(DEPTH):
                link(dve.tensor_tensor(lower_all[:, d, :], lbp[:, d, :], top, ALU.subtract))
            dve.sem_inc(sem("lb_shifted"), 1)
            dve.wait_ge(sem("lb_exp"), 1)
            link(dve.tensor_copy(top, lbp[:, 0, :]))
            for d in range(1, DEPTH):
                link(dve.tensor_tensor(top, top, lbp[:, d, :], ALU.add))
            link(dve.reciprocal(top, top))
            for d in range(DEPTH):
                link(dve.tensor_tensor(lbp[:, d, :], lbp[:, d, :], top, ALU.mult))
            link(dve.tensor_copy(lower_all[:, 0, :], lbp[:, 0, :]))
            for d in range(1, DEPTH):
                link(dve.tensor_tensor(lower_all[:, d, :], lower_all[:, d - 1, :], lbp[:, d, :], ALU.add))
            for d in range(DEPTH):
                link(dve.tensor_tensor(lower_all[:, d, :], lower_all[:, d, :], lbp[:, 0, :], ALU.subtract))

            dve.wait_ge(sem("mem_rooted"), 1)
            link(dve.reciprocal(minv[:, :], minv[:, :]))

            def scaled(n, gain, done, then=None):
                dve.wait_ge(sem("rooted"), n + 1)
                dve.reciprocal(rinv[:, :], rinv[:, :]).then_inc(sem("inverted"), 1)
                dve.wait_ge(sem("inverted"), n + 1)
                for k in range(KC):
                    dve.scalar_tensor_tensor(h[:, k, :], x[:, k, :], gain[:, k:k + 1], rinv[:, :],
                                             ALU.mult, ALU.mult).then_inc(sem(done), 1)
                    if k and then:
                        then(k - 1)
                if then:
                    then(KC - 1)

            with dve.Fori(0, DEPTH) as l:
                chained = [0]

                def link(ins):
                    chained[0] += 1
                    ins.then_inc(sem("chain"), 1)
                    dve.wait_ge(sem("chain"), l * CHAIN + chained[0])

                def ev(name, n=1, per=1):
                    dve.wait_ge(sem(name), l * per + n)

                def settle():
                    dve.sem_inc(sem("settled"), 1)

                def out_of_banks(n):
                    dve.wait_ge(sem("bank_free"), l * TILES + n + 2)

                def low_of(dst, src, hi, high, at, per, done):
                    ev(high, at, per)
                    dve.tensor_tensor(dst, src, hi, ALU.subtract).then_inc(sem(done), 1)

                def normalised(n, gain):
                    def low(k):
                        low_of(hr[1][:, k, :], h[:, k, :], hr[0][:, k, :], "h_high", n * KC + k + 1, 3 * KC, "h_ready")

                    scaled(l * 3 + n, gain, "h_made", low)

                link(dve.tensor_copy(small[:, :], smalls[:, bass.ds(l, 1), :].rearrange("p a n -> p (a n)")))
                link(dve.tensor_copy(low[:, :], lower_all[:, bass.ds(l, 1), :].rearrange("p a n -> p (a n)")))
                link(dve.tensor_scalar(oml[:, :], low[:, :], -1.0, 1.0, ALU.mult, ALU.add))
                gain = {k: small[:, n:n + KC] for k, n in gains.items()}
                normalised(0, gain["mix"])

                ev("rope_tables", 32, 32)
                link(dve.tensor_copy(posf, posi))
                two_pi = 2 * np.pi
                c1 = 6.28125
                c2 = float(np.float32(two_pi - c1).view(np.uint32).__and__(np.uint32(0xFFFFF000)).view(np.float32))
                c3 = float(np.float32(two_pi - c1 - c2))
                magic = 1.5 * 2.0 ** 23
                pi = float(np.nextafter(np.float32(np.pi), np.float32(0)))
                for n in range(2):
                    link(dve.tensor_scalar(ang, posf, freq[:, n:n + 1], None, ALU.mult))
                    for dst, quarter in ((sinb, 0.0), (cosb, 0.25)):
                        link(dve.tensor_scalar(turn, ang, 1 / two_pi, quarter, ALU.mult, ALU.add))
                        link(dve.tensor_scalar(turn, turn, magic, None, ALU.add))
                        link(dve.tensor_scalar(turn, turn, magic, None, ALU.subtract))
                        link(dve.scalar_tensor_tensor(red, turn, -c1, ang, ALU.mult, ALU.add))
                        link(dve.scalar_tensor_tensor(red, turn, -c2, red, ALU.mult, ALU.add))
                        link(dve.scalar_tensor_tensor(red, turn, -c3, red, ALU.mult, ALU.add))
                        link(dve.tensor_scalar(red, red, quarter * two_pi, pi, ALU.add, ALU.min))
                        dve.tensor_scalar(dst[:, n, :], red, -pi, None, ALU.max).then_inc(sem("angles"), 1)
                        ev("angles", 2 * n + (1 if quarter == 0 else 2), 4)

                def rope(dst, rotated, tmp, n, tiles):
                    link(dve.tensor_tensor(tmp, rotated, bc(sinb[:, n, :], 1, tiles), ALU.mult))
                    link(dve.tensor_tensor(dst, dst, bc(cosb[:, n, :], 1, tiles), ALU.mult))
                    return dve.tensor_tensor(dst, dst, tmp, ALU.add)

                out_of_banks(T_RV)
                ev("trig", 2, 2)
                ev("ret_rotated", 1, 2)
                link(rope(rq, pview(0, 2, "p (h t) -> p h t", h=HEADS), rtmp, 0, HEADS))
                ev("ret_rotated", 2, 2)
                rope(rk, pview(2, 2, "p (h t) -> p h t", h=HEADS), rtmp, 0, HEADS).then_inc(sem("ret_roped"), 1)
                ev("ret_sig")
                link(dve.tensor_tensor(rgs, rgs, rg, ALU.mult))
                ev("ret_scored")
                out_of_banks(T_SQ)
                ev("tables", 48, 48)
                dve.tensor_tensor(st, bank[:, 0:4, 0:3 * P], decay, ALU.mult).then_inc(sem("ret_decayed"), 1)
                out_of_banks(T_HF)
                ev("win_rotated")
                rope(wqk, pview(0, 3, "p (h t) -> p h t", h=6)[:, 0:5, :], wtmp, 1, 5).then_inc(sem("win_roped"), 1)
                ev("ret_rooted")
                link(dve.reciprocal(rrms, rrms))
                link(dve.tensor_tensor(rrms, rrms, pview(6, 2, "p (h t) -> p h t", h=HEADS), ALU.mult))
                dve.tensor_tensor(rrms, rrms, rgs, ALU.mult).then_inc(sem("ret_out"), 1)
                low_of(branch_r[1][:, 0, :, :], rrms, branch_r[0][:, 0, :, :], "branch_high", 1, 4, "branch_low")

                mx2 = mx[:, :].rearrange("p (j t) -> p j t", t=2)

                def window_low(half):
                    p0 = half * SWA_DIM
                    low_of(branch_r[1][p0:p0 + SWA_DIM, 1, :, :],
                           pview(6, 2, "p (h t) -> p h t", h=4)[p0:p0 + SWA_DIM],
                           branch_r[0][p0:p0 + SWA_DIM, 1, :, :], "branch_high", 2 + half, 4, "branch_low")

                for half in range(2):
                    ev("win_scored", half + 1, 2)
                    link(dve.scalar_tensor_tensor(wp, bank[:, 0:4, 0:3 * P], SWA_DIM ** -0.5, bc(window, 1, 4),
                                                  ALU.mult, ALU.add))
                    link(dve.tensor_reduce(mx2[:, :, 0], wp[:, :, 0:P], AX.X, ALU.max))
                    link(dve.tensor_reduce(mx2[:, :, 1], wp[:, :, P:3 * P], AX.X, ALU.max))
                    sk = bc(sink[:, half * 4:half * 4 + 4], 2, 2)
                    link(dve.tensor_tensor(mx2, mx2, sk, ALU.max))
                    link(dve.tensor_tensor(esink[:, :].rearrange("p (j t) -> p j t", t=2), sk, mx2, ALU.subtract))
                    dve.tensor_scalar(negm[:, :], mx[:, :], -1.0, None, ALU.mult).then_inc(sem("win_max"), 1)
                    if half:
                        window_low(0)
                    ev("win_exp", 9 * (half + 1), 18)
                    link(dve.tensor_tensor(rsum[:, :], rsum[:, :], esink[:, :], ALU.add))
                    link(dve.reciprocal(rsum[:, :], rsum[:, :]))
                    rs2 = rsum[:, :].rearrange("p (j t) -> p j t", t=2)
                    link(dve.tensor_tensor(wp[:, :, 0:P], wp[:, :, 0:P], bc(rs2[:, :, 0], 2, P), ALU.mult))
                    dve.tensor_tensor(wp[:, :, P:3 * P], wp[:, :, P:3 * P], bc(rs2[:, :, 1], 2, 2 * P), ALU.mult
                                      ).then_inc(sem("win_probs"), 1)

                ev("hgrn_sig", 4, 4)
                c3d = cum.rearrange("p (h t) -> p h t", h=HEADS)
                k3d = kin.rearrange("p (h t) -> p h t", h=HEADS)
                for hd in range(HEADS):
                    dve.tensor_scalar(c3d[:, hd, :], c3d[:, hd, :], oml[:, hd:hd + 1], low[:, hd:hd + 1],
                                      ALU.mult, ALU.add)
                    link(dve.tensor_scalar(k3d[:, hd, :], k3d[:, hd, :], oml[:, hd:hd + 1], None, ALU.mult))
                link(dve.tensor_scalar(cum, cum, TINY, None, ALU.max))
                link(dve.scalar_tensor_tensor(qin, hq.rearrange("p h t -> p (h t)"), P ** -0.5, qin, ALU.mult, ALU.mult))
                link(dve.tensor_scalar(small_f, cum, 2.0 ** -40, 2.0 ** 60, ALU.is_lt, ALU.mult))
                dve.scalar_tensor_tensor(cum, small_f, 1.0, cum, ALU.max, ALU.mult).then_inc(sem("forget"), 1)
                dve.sem_inc(sem("level_ready"), 1)
                ev("log_forget")
                link(dve.scalar_tensor_tensor(cum, small_f, float(-60 * np.log(2.0) / 2.0 ** 60), cum,
                                              ALU.mult, ALU.add))
                st2 = st.rearrange("p h (n t) -> p h n t", n=3)[:, :, 0:3:2, :]
                scored = pview(0, 2, "p (h n t) -> p h n t", h=HEADS, n=2)

                def halves(v, m):
                    return v.rearrange("p (b s m) -> p b s m", s=2, m=m)

                def span_of(m):
                    c = halves(cum, m)
                    dve.tensor_tensor(halves(span, m)[:, :, 0, :], bc(c[:, :, 0, m - 1], 2, m), c[:, :, 0, :],
                                      ALU.subtract).then_inc(sem("span_ready"), 1)

                def take_level(i):
                    ev("level_scored", i + 1, 9)
                    if i == 0:
                        return dve.tensor_tensor(st2, scored, bc(bc(ident[:, :], 1, 2), 1, HEADS), ALU.mult)
                    settle()
                    return dve.copy_predicated(st2, bc(bc(level_mask[:, i - 1, :], 1, 2), 1, HEADS), scored)

                span_of(1)
                window_low(1)
                link(take_level(0))
                link(dve.tensor_tensor(hgs, hgs, hg, ALU.mult))
                for hd in range(HEADS):
                    ins = dve.tensor_scalar(hgs[:, hd, :], hgs[:, hd, :], hgain[:, hd:hd + 1], None, ALU.mult)
                link(ins)
                for i, m in enumerate(LEVELS):
                    if i == 0:
                        continue
                    if i > 1:
                        link(take_level(i - 1))
                    ev("level_exp", 2 * i, 16)
                    dve.tensor_tensor(halves(left, m)[:, :, 0, :], halves(kin, m)[:, :, 0, :],
                                      halves(span, m)[:, :, 0, :], ALU.mult)
                    link(dve.tensor_tensor(halves(right, m)[:, :, 1, :], halves(qin, m)[:, :, 1, :],
                                           halves(span, m)[:, :, 1, :], ALU.mult))
                    dve.sem_inc(sem("level_ready"), 1)
                    if i < 8:
                        c = halves(cum, m)
                        link(dve.tensor_tensor(c[:, :, 1, :], c[:, :, 1, :], bc(c[:, :, 0, m - 1], 2, m), ALU.add))
                        span_of(2 * m)
                dve.sem_inc(sem("hgrn_scores"), 1)

                def low_mixed(s):
                    low_of(hr[1][:, 2 * s:2 * s + 2, :], mixed[:, 2 * s:2 * s + 2, :], hr[0][:, 2 * s:2 * s + 2, :],
                           "mixed_high", s + 1, SLOTS, "mixed_low")

                def gate_branch(b, tiles=range(SLOTS)):
                    g0 = GATES_OF[b]
                    ev("gates_ready", b + 1, 3)
                    for s in tiles:
                        used(dve, l * GROUPS + G_BR + b, s)
                        y = bank[:, 4 + s % 2, :].rearrange("p (j t) -> p j t", j=2)
                        g = gates[:, g0 + 2 * s:g0 + 2 * s + 2, :]
                        o = mixed[:, 2 * s:2 * s + 2, :]
                        if b == 0:
                            dve.tensor_tensor(o, y, g, ALU.mult).then_inc(sem("bank_free"), 1)
                        else:
                            dve.tensor_tensor(g, y, g, ALU.mult).then_inc(sem("bank_free"), 1)
                            out_of_banks(T_BR + 4 * b + s + 1)
                            if b == 2:
                                dve.wait_ge(sem("mixed_ready"), l * 2 * SLOTS + s + 1)
                            dve.tensor_tensor(o, o, g, ALU.add).then_inc(sem("mixed_ready"), 1)
                            if b == 2 and s:
                                low_mixed(s - 1)

                gate_branch(0)
                gate_branch(1, (0, 1))
                ev("hgrn_rooted")
                link(dve.reciprocal(rinv[:, :], rinv[:, :]))
                link(dve.tensor_tensor(hgo, pview(6, 2, "p (h t) -> p h t", h=HEADS), bc(rinv[:, :], 1, HEADS), ALU.mult))
                dve.tensor_tensor(hgo, hgo, hgs, ALU.mult).then_inc(sem("hgrn_out"), 1)
                low_of(branch_r[1][:, 2, :, :], hgo, branch_r[0][:, 2, :, :], "branch_high", 4, 4, "branch_low")
                gate_branch(1, (2, 3))
                ev("mem_loaded", 16, 16)
                for k in range(KC):
                    dve.scalar_tensor_tensor(mem[:, k, :], mem[:, k, :], gain["xkv"][:, k:k + 1], minv[:, :],
                                             ALU.mult, ALU.mult).then_inc(sem("mn_made"), 1)
                gate_branch(2)
                low_mixed(SLOTS - 1)
                for k in range(KC):
                    low_of(mn_r[1][:, k, :], mem[:, k, :], mn_r[0][:, k, :], "mn_high", k + 1, KC, "mn_low")

                def add_tiles(g0, n0):
                    with dve.Fori(0, 2) as i:
                        for s in range(SLOTS):
                            used(dve, l * GROUPS + g0 + i, s)
                            o = x[:, bass.ds(i * SLOTS + s, 1), :].rearrange("p a t -> p (a t)")
                            dve.tensor_tensor(o, o, tile_out(s), ALU.add).then_inc(sem("bank_free"), 1)
                    out_of_banks(n0 + 2 * SLOTS)
                    dve.sem_inc(sem("x_ready"), 1)

                settle()
                add_tiles(G_OUT, T_OUT)
                normalised(1, gain["xq"])

                ev("x_scored")
                link(dve.tensor_reduce(mx[:, :], four.rearrange("p b (c m) -> p (b c) m", c=2), AX.X, ALU.max))
                dve.tensor_scalar(negm[:, :], mx[:, :], -(2 * P) ** -0.5, None, ALU.mult).then_inc(sem("x_max"), 1)
                ev("x_exp", 8, 8)
                link(dve.reciprocal(rsum[:, :], rsum[:, :]))
                dve.tensor_tensor(xp, xp, bc(rsum[:, :], 2, N_MEM), ALU.mult).then_inc(sem("x_probs"), 1)
                low_of(xo_r[1], four.rearrange("p b (c m) -> p (b c) m", c=2), xo_r[0], "xo_high", 1, 1, "xo_low")
                settle()
                add_tiles(G_XO, T_XO)
                normalised(2, gain["ffn"])

                def top16(rows, read=None):
                    def every(op):
                        for row in rows:
                            m = op(*row)
                        link(m)

                    settle()
                    every(lambda vals, ids, data, work: dve.max(out=vals[:, 0:8], in_=data))
                    settle()
                    for vals, ids, data, work in rows:
                        dve.max_index(ids[:, 0:8], vals[:, 0:8], data)
                    every(lambda vals, ids, data, work: dve.match_replace(
                        out=work, in_to_replace=vals[:, 0:8], in_values=data, imm_value=-3e38))
                    if read:
                        dve.sem_inc(sem(read), 1)
                    settle()
                    every(lambda vals, ids, data, work: dve.max(out=vals[:, 8:16], in_=work))
                    settle()
                    every(lambda vals, ids, data, work: dve.max_index(ids[:, 8:16], vals[:, 8:16], work))

                for q in range(4):
                    ev("keys_out", q + 3, 4)
                    top16([(best[:, t, 2 * q + k // 2, k % 2, :], idx[:, t, 2 * q + k // 2, k % 2, :],
                            kscore[:, q % 2, t, k, :], work[:, t, k, :]) for t in range(NT) for k in range(SLOTS)],
                          "keys_read")
                for t in range(NT):
                    link(dve.tensor_copy(idxb[:, t], idx[:, t]))
                    link(dve.tensor_tensor(cand.rearrange("p h (i j) -> p h i j", i=TOPK),
                                           bc(best[:, t, :, 0, :], 3, TOPK), bc(best[:, t, :, 1, :], 2, TOPK), ALU.add))
                    top16([(cbest[:, t, hd], cidx[:, hd], cand[:, hd], candw[:, hd]) for hd in range(PH)])
                    link(dve.tensor_copy(gsum[:, t], cbest[:, t, :, 0]))
                    dve.tensor_tensor(cbest[:, t], cbest[:, t], bc(gsum[:, t], 2, TOPK), ALU.subtract
                                      ).then_inc(sem("cand_max"), 1)
                    cflat = cidx.rearrange("p h k -> p (h k)")
                    dve.tensor_single_scalar(cij[:, 0, :], cflat, 4, ALU.logical_shift_right)
                    link(dve.tensor_single_scalar(cij[:, 1, :], cflat, 15, ALU.bitwise_and))
                    link(dve.tensor_copy(cijb, cij))
                    for side in range(2):
                        link(dve.tensor_tensor(hot, bc(cijb[:, side, :], 2, TOPK), bc(iota[:, 0:TOPK], 1, P), ALU.is_equal))
                        hot4 = hot.rearrange("p (h k) i -> p h k i", h=PH)
                        link(dve.tensor_tensor(hot4, hot4, bc(idxb[:, t, :, side, :], 2, TOPK), ALU.mult))
                        link(dve.tensor_reduce(sel[:, t, side, :], hot, AX.X, ALU.add))
                ev("cand_exp")
                link(dve.tensor_reduce(gsum, cbest, AX.X, ALU.add))
                link(dve.reciprocal(gsum, gsum))
                for t in range(NT):
                    dve.tensor_tensor(sel[:, t, 2, :].rearrange("p (h k) -> p h k", h=PH), cbest[:, t],
                                      bc(gsum[:, t], 2, TOPK), ALU.mult).then_inc(sem("selected"), 1)

                ev("sel_turned_out", 2, 2)
                link(dve.tensor_copy(pair12[:, :, :], selT[:, 0:2, :]))
                for c in range(3):
                    link(dve.tensor_copy(gate3[:, :, c], selT[:, 2, :]))
                    if c < 2:
                        link(dve.tensor_tensor(selT[:, 2, :], selT[:, 2, :], gate3[:, :, c], ALU.subtract))

                def one_hots(j, parity, b0, t0, shared=False):
                    dve.wait_ge(sem("spread"), l * NK + j + 1)
                    tok = bass.ds(t0, TOK)
                    dve.tensor_tensor(equal2[:, parity, :, :], bc(iota[:, b0:b0 + QB], 1, TOK),
                                      bc(pair12[:, 1, tok], 2, QB), ALU.is_equal).then_inc(sem("equal2"), 1)
                    ins = dve.tensor_tensor(one1[:, parity, :, :], bc(iota[:, :], 1, TOK), bc(pair12[:, 0, tok], 2, P),
                                            ALU.is_equal)
                    if not shared:
                        dve.wait_ge(sem("equal2"), l * NK + j + 1)
                        ins = dve.tensor_tensor(one2[:, parity, :, :, :], bc(equal2[:, parity, :, :], 2, 3),
                                                bc(gate3[:, tok, :], 3, QB), ALU.mult)
                    ins.then_inc(sem("hot_ready"), 1)

                settle()
                with dve.Fori(0, QB // 2) as i:
                    for r in range(2):
                        one_hots(i * 2 + r, r, 0, (i * 2 + r) * TOK, shared=True)
                one_hots(QB, 0, QB, 0)
                one_hots(QB + 1, 1, QB, TOK)

                def multiply(m, parity, slot, gslot, g, s):
                    dve.wait_ge(sem("up_free"), l * NK + m + 3)
                    used(dve, l * GROUPS + g, s)
                    dve.wait_ge(sem("gated"), l * NK + m + 1)
                    dve.tensor_tensor(product, actv[:, bass.ds(slot, 1), :].rearrange("p a t -> p (a t)"),
                                      G[:, bass.ds(gslot, 1), :].rearrange("p a t -> p (a t)"), ALU.mult
                                      ).then_inc(sem("multiplied"), 1)

                def gated_low(m, parity):
                    dve.wait_ge(sem("gated_high"), l * NK + m + 1)
                    dve.tensor_tensor(gated_r[1][:, parity, :], product, gated_r[0][:, parity, :],
                                      ALU.subtract).then_inc(sem("gated"), 1)

                dve.wait_ge(sem("spread_free"), l * NK + QB + 3)
                multiply(0, 0, 0, 0, G_MAIN - 1, 3)
                gated_low(0, 0)

                def main(q, i, last):
                    n0 = q * QB + i * 2
                    g = G_MAIN + q * (QB // 2) + i
                    for r in range(2):
                        over = last and r == 1
                        if not (q == QUARTERS - 2 and last):
                            b = q + 2 if last else q + 1
                            one_hots(QB + 2 + n0 + r, r, b * QB, r * TOK if last else (i * 2 + r + 2) * TOK)
                        dve.wait_ge(sem("spread_free"), l * NK + QB + n0 + r + 3)
                        slot = 0 if over else i * 2 + r + 1
                        multiply(n0 + r + 1, 1 - r, slot, (((q + 1) if over else q) % 2) * QB + slot,
                                 g - 1 + r, 3 - 2 * r)
                        gated_low(n0 + r + 1, 1 - r)

                settle()
                for q in range(QUARTERS - 1):
                    with dve.Fori(0, QB // 2 - 1) as i:
                        main(q, i, False)
                    main(q, QB // 2 - 1, True)
                    settle()

                def tail(i, last):
                    for s in range(SLOTS):
                        m = NK - QB + i * SLOTS + s + 1
                        if not (last and s == SLOTS - 1):
                            g, before = (G_TAIL + i - 1, 3) if s == 0 else (G_TAIL + i, s - 1)
                            multiply(m, (s + 1) % 2, i * SLOTS + s + 1, QB + i * SLOTS + s + 1, g, before)
                            gated_low(m, (s + 1) % 2)

                with dve.Fori(0, QB // SLOTS - 1) as i:
                    tail(i, False)
                tail(QB // SLOTS - 1, True)
                for s in range(SLOTS):
                    used(dve, l * GROUPS + GROUPS - 1, s)
                dve.tensor_tensor(x[:, :, :], x[:, :, :], four.rearrange("p b (c t) -> p (b c) t", c=2), ALU.add
                                  ).then_inc(sem("x_ready"), 1)
                assert chained[0] == CHAIN, chained[0]

            scaled(DEPTH * 3, gfin, "final")


def kernel(x, mem, positions, ln_mix, w_in, lb_param, hgrn_norm, swa_sinks, w_br_hgrn, w_br_ret, w_br_swa, w_out,
           ln_xq, ln_xkv, w_xq, w_xk, w_xv, w_xo, ln_ffn, peer_wq, peer_keys, peer_u, peer_v, ln_final):
    import concourse.bacc as bacc
    from concourse.bass_utils import run_bass_kernel_spmd

    f = np.float32

    def by_chunk(v):
        v = np.asarray(v)
        return np.ascontiguousarray(v.reshape(v.shape[:-1] + (-1, P)).swapaxes(-1, -2))

    def tiles(w):
        rows, cols = w.shape
        return w.reshape(rows // P, P, cols // P, P).transpose(2, 1, 0, 3).reshape(cols // P, P, -1)

    stream = np.empty(((DEPTH * GROUPS + 1) * SLOTS, P, D), f)
    keys = np.empty((DEPTH, P, 2 * PH, NK), f)
    pair = np.concatenate([np.r_[j * SWA_DIM:(j + 1) * SWA_DIM, (j + 4) * SWA_DIM:(j + 5) * SWA_DIM] for j in range(4)])
    for l in range(DEPTH):
        out = stream[l * GROUPS * SLOTS:(l + 1) * GROUPS * SLOTS]

        def put(g, t, s=0):
            out[g * SLOTS + s:g * SLOTS + s + len(t)] = t

        w = np.asarray(w_in[l])
        hq, hf, hi, hg, rq, rk, rv, rg, sq, sk, sv, gl = np.split(w, np.cumsum([512] * 9 + [P, P]), axis=1)
        for g, part in ((G_RQ, rq), (G_RK, rk), (G_RV, rv), (G_RG, rg), (G_SQ, sq[:, pair]), (G_HF, hf), (G_HQ, hq),
                        (G_HI, hi), (G_HG, hg), (G_GATE, gl), (G_XK, w_xk[l]), (G_XV, w_xv[l]), (G_OUT, w_out[l]),
                        (G_XQ, w_xq[l]), (G_XO, w_xo[l]), (G_WQ, peer_wq[l])):
            put(g, tiles(np.asarray(part)))
        for s, part in enumerate((sv, sv, sk, sk)):
            put(G_SKV, tiles(part), s)
        for b, part in enumerate((w_br_ret[l], np.asarray(w_br_swa[l])[pair], w_br_hgrn[l])):
            t = tiles(np.asarray(part)).reshape(4, 2, P, 512).transpose(0, 2, 1, 3).reshape(4, P, D)
            put(G_BR + b, t)
        keys[l] = np.asarray(peer_keys[l]).transpose(3, 1, 0, 2).reshape(P, 2 * PH, NK)
        u = np.asarray(peer_u[l]).reshape(NK, NK, KC, P).transpose(1, 3, 2, 0).reshape(NK, P, D)
        v = np.asarray(peer_v[l]).reshape(NK, NK, D).transpose(1, 0, 2)
        put(G_AHEAD, u[:QB])
        m = out[G_MAIN * SLOTS:G_TAIL * SLOTS].reshape(N_MAIN, SLOTS, P, D)
        m[:, 0::2] = u[QB:].reshape(N_MAIN, 2, P, D)
        m[:, 1::2] = v[:NK - QB].reshape(N_MAIN, 2, P, D)
        put(G_TAIL, v[NK - QB:])
    stream[DEPTH * GROUPS * SLOTS:] = stream[:SLOTS]

    small = np.concatenate(
        [by_chunk(v) for v in (ln_mix, ln_xq, ln_xkv, ln_ffn, hgrn_norm)]
        + [np.broadcast_to(np.asarray(swa_sinks)[:, None, :], (DEPTH, P, 8))], axis=2)
    arrays = {
        "x": np.ascontiguousarray(np.asarray(x)[0].reshape(T, KC, P).transpose(2, 1, 0)),
        "mem": np.ascontiguousarray(np.asarray(mem)[0].reshape(N_MEM, KC, P).transpose(2, 1, 0)),
        "pos": np.asarray(positions),
        "small": np.ascontiguousarray(small.transpose(1, 0, 2)),
        "lb": np.ascontiguousarray(by_chunk(lb_param).transpose(1, 0, 2)),
        "gfin": by_chunk(ln_final),
        "stream": stream,
        "keys": keys,
        **lay_constants(),
    }
    nc = bacc.Bacc("TRN2", target_bir_lowering=False, num_devices=1)
    aps = {n: nc.dram_tensor(f"in_{n}", v.shape, mybir.dt.from_np(v.dtype), kind="ExternalInput").ap()
           for n, v in arrays.items()}
    aps["out"] = nc.dram_tensor("out_dram", (P, KC, T), F32, kind="ExternalOutput").ap()
    build(nc, aps)
    r = run_bass_kernel_spmd(nc, [{f"in_{n}": v for n, v in arrays.items()}], core_ids=[0])
    y = r.results[0]["out_dram"]
    return np.ascontiguousarray(y.transpose(2, 1, 0)).reshape(1, T, D)
```
